# Optimizing a Trainium2 kernel written in Bass

```python
import math, functools
import jax, jax.numpy as jnp
from jax import lax
import numpy as np

D_MODEL = 2048
BATCH = 1
SEQ = 256
DEPTH = 1
DEC_BATCH = 8
DEC_SEQ = 1
PAST_LEN = 2048
PAGE_SIZE = 128

CONV_WIDTH = D_MODEL // 2
RET_WIDTH = D_MODEL - CONV_WIDTH
RET_HEADS = 8
RET_HEAD_DIM = RET_WIDTH // RET_HEADS
CONV_K = 3
RET_CHUNK = 128
ROPE_BASE = 10000.0
IN_WIDTH = 3 * CONV_WIDTH + 4 * RET_WIDTH
PEER_HEADS = 8
PEER_NKEYS = 128
PEER_N = PEER_NKEYS * PEER_NKEYS
PEER_QDIM = 256
PEER_HALF = PEER_QDIM // 2
PEER_TOPK = 16
PEER_TOKEN_BLOCK = 128
EPS = 1e-6
GN_EPS = 1e-5

kernel_name = "hymba_conv_retention_peer_step"

def rmsnorm(x, g):
    xf = x.astype(jnp.float32)
    y = xf * lax.rsqrt(jnp.mean(xf * xf, axis=-1, keepdims=True) + EPS) * g.astype(jnp.float32)
    return y.astype(x.dtype)

def rotary(x, pos):
    half = x.shape[-1] // 2
    inv = ROPE_BASE ** (-jnp.arange(half, dtype=jnp.float32) / half)
    ang = pos.astype(jnp.float32)[:, None] * inv[None, :]
    cos = jnp.cos(ang)[None, :, None, :]
    sin = jnp.sin(ang)[None, :, None, :]
    x1, x2 = x[..., :half], x[..., half:]
    return jnp.concatenate([x1 * cos - x2 * sin, x1 * sin + x2 * cos], axis=-1)

def retention(q, k, v, s0):
    b, t, nh, d = q.shape
    c = math.gcd(t, RET_CHUNK)
    n = t // c
    log_g = jnp.log(1.0 - 2.0 ** (-5.0 - jnp.arange(nh, dtype=jnp.float32)))
    i = jnp.arange(c, dtype=jnp.float32)
    diff = i[:, None] - i[None, :]
    decay = jnp.where(diff[None] >= 0, jnp.exp(jnp.maximum(diff, 0.0)[None] * log_g[:, None, None]), 0.0)
    xi = jnp.exp((i[:, None] + 1.0) * log_g[None, :])
    zeta = jnp.exp((c - 1.0 - i[:, None]) * log_g[None, :])
    g_c = jnp.exp(c * log_g)

    def to_chunks(a):
        return a.reshape(b, n, c, nh, d).transpose(1, 0, 2, 3, 4)

    def step(s, blk):
        qc, kc, vc = blk
        sc = jnp.einsum('bnhd,bmhd->bhnm', qc, kc) * decay[None]
        o_in = jnp.einsum('bhnm,bmhe->bnhe', sc, vc)
        o_cross = jnp.einsum('bnhd,bhde->bnhe', qc, s) * xi[None, :, :, None]
        s_new = g_c[None, :, None, None] * s + jnp.einsum('bmhd,bmhe->bhde', kc * zeta[None, :, :, None], vc)
        return s_new, o_in + o_cross

    s_fin, out = lax.scan(step, s0, (to_chunks(q), to_chunks(k), to_chunks(v)))
    out = out.transpose(1, 0, 2, 3, 4).reshape(b, t, nh, d)
    return out, s_fin

def mixer(h, conv_buf, ret_state, pos, w_in, conv_w, ret_gn_g, ret_gn_b, w_out):
    b, t, _ = h.shape
    proj = jnp.einsum('btd,de->bte', h, w_in)
    cuts = [CONV_WIDTH, 2 * CONV_WIDTH, 3 * CONV_WIDTH,
            3 * CONV_WIDTH + RET_WIDTH, 3 * CONV_WIDTH + 2 * RET_WIDTH, 3 * CONV_WIDTH + 3 * RET_WIDTH]
    bg, cg, hc, q, k, v, g = jnp.split(proj, cuts, axis=-1)
    u = cg * hc
    full = jnp.concatenate([conv_buf.astype(u.dtype), u], axis=1)
    conv_out = sum([full[:, j:j + t] * conv_w[j] for j in range(CONV_K)])
    y_conv = bg * conv_out
    new_buf = full[:, t:]
    qh = rotary(q.reshape(b, t, RET_HEADS, RET_HEAD_DIM).astype(jnp.float32), pos)
    kh = rotary(k.reshape(b, t, RET_HEADS, RET_HEAD_DIM).astype(jnp.float32), pos) * (RET_HEAD_DIM ** -0.5)
    vh = v.reshape(b, t, RET_HEADS, RET_HEAD_DIM).astype(jnp.float32)
    o, s_new = retention(qh, kh, vh, ret_state.astype(jnp.float32))
    mu = jnp.mean(o, axis=-1, keepdims=True)
    var = jnp.mean(jnp.square(o - mu), axis=-1, keepdims=True)
    o = ((o - mu) * lax.rsqrt(var + GN_EPS)).reshape(b, t, RET_WIDTH)
    o = o * ret_gn_g.astype(jnp.float32) + ret_gn_b.astype(jnp.float32)
    y_ret = (jax.nn.silu(g.astype(jnp.float32)) * o).astype(h.dtype)
    y = jnp.concatenate([y_conv, y_ret], axis=-1)
    out = jnp.einsum('bte,ed->btd', y, w_out)
    return out, new_buf.astype(conv_buf.dtype), s_new.astype(ret_state.dtype)

def peer(h, w_q, sub_keys, u_tab, v_tab):
    b, t, d = h.shape
    nt = b * t
    blk = math.gcd(nt, PEER_TOKEN_BLOCK)
    xb_all = h.reshape(nt // blk, blk, d)

    def block(xb):
        q = jnp.einsum('td,de->te', xb, w_q).reshape(blk, PEER_HEADS, 2, PEER_HALF).astype(jnp.float32)
        sc = jnp.einsum('thcd,hckd->thck', q, sub_keys.astype(jnp.float32))
        v1, i1 = lax.top_k(sc[:, :, 0], PEER_TOPK)
        v2, i2 = lax.top_k(sc[:, :, 1], PEER_TOPK)
        cand = (v1[..., :, None] + v2[..., None, :]).reshape(blk, PEER_HEADS, PEER_TOPK * PEER_TOPK)
        cidx = (i1[..., :, None] * PEER_NKEYS + i2[..., None, :]).reshape(blk, PEER_HEADS, PEER_TOPK * PEER_TOPK)
        best, pos = lax.top_k(cand, PEER_TOPK)
        idx = jnp.take_along_axis(cidx, pos, axis=-1)
        gate = jax.nn.softmax(best, axis=-1)
        u = u_tab[idx]
        act = jax.nn.gelu(jnp.einsum('td,thkd->thk', xb, u).astype(jnp.float32), approximate=False)
        w = (gate * act).astype(xb.dtype)
        return jnp.einsum('thk,thkd->td', w, v_tab[idx])

    return lax.map(block, xb_all).reshape(b, t, d)

def trunk(x, conv_bufs, ret_states, pos, norm_mix_g, w_in, conv_w, ret_gn_g, ret_gn_b, w_out,
          norm_ffn_g, peer_w_q, peer_sub_keys, peer_u, peer_v, norm_final_g):
    new_conv, new_ret = [], []
    for l in range(DEPTH):
        mix, cb, rs = mixer(rmsnorm(x, norm_mix_g[l]), conv_bufs[l], ret_states[l], pos,
                            w_in[l], conv_w[l], ret_gn_g[l], ret_gn_b[l], w_out[l])
        x = x + mix
        x = x + peer(rmsnorm(x, norm_ffn_g[l]), peer_w_q[l], peer_sub_keys[l], peer_u[l], peer_v[l])
        new_conv.append(cb)
        new_ret.append(rs)
    return rmsnorm(x, norm_final_g), jnp.stack(new_conv), jnp.stack(new_ret)

def setup_inputs(seed: int = 0) -> dict:
    key = jax.random.key(seed)
    ks = jax.random.split(key, 16)
    f32 = jnp.float32
    nrm = lambda k, s, sc: jax.random.normal(k, s, f32) * sc
    return {
        'x_prompt': nrm(ks[0], (BATCH, SEQ, D_MODEL), 1.0),
        'x_sample': nrm(ks[1], (DEC_BATCH, DEC_SEQ, D_MODEL), 1.0),
        'state_conv': nrm(ks[2], (DEPTH, DEC_BATCH, CONV_K - 1, CONV_WIDTH), 1.0),
        'state_ret': nrm(ks[3], (DEPTH, DEC_BATCH, RET_HEADS, RET_HEAD_DIM, RET_HEAD_DIM), 1.0),
        'norm_mix_g': 1.0 + nrm(ks[4], (DEPTH, D_MODEL), 0.02),
        'w_in': nrm(ks[5], (DEPTH, D_MODEL, IN_WIDTH), D_MODEL ** -0.5),
        'conv_w': nrm(ks[6], (DEPTH, CONV_K, CONV_WIDTH), CONV_K ** -0.5),
        'ret_gn_g': 1.0 + nrm(ks[7], (DEPTH, RET_WIDTH), 0.02),
        'ret_gn_b': nrm(ks[8], (DEPTH, RET_WIDTH), 0.02),
        'w_out': nrm(ks[9], (DEPTH, D_MODEL, D_MODEL), D_MODEL ** -0.5),
        'norm_ffn_g': 1.0 + nrm(ks[10], (DEPTH, D_MODEL), 0.02),
        'peer_w_q': nrm(ks[11], (DEPTH, D_MODEL, PEER_HEADS * PEER_QDIM), D_MODEL ** -0.5),
        'peer_sub_keys': nrm(ks[12], (DEPTH, PEER_HEADS, 2, PEER_NKEYS, PEER_HALF), PEER_HALF ** -0.5),
        'peer_u': nrm(ks[13], (DEPTH, PEER_N, D_MODEL), D_MODEL ** -0.5),
        'peer_v': nrm(ks[14], (DEPTH, PEER_N, D_MODEL), PEER_HEADS ** -0.5),
        'norm_final_g': 1.0 + nrm(ks[15], (D_MODEL,), 0.02),
    }

def reference(x_prompt, x_sample, state_conv, state_ret, norm_mix_g, w_in, conv_w, ret_gn_g, ret_gn_b,
              w_out, norm_ffn_g, peer_w_q, peer_sub_keys, peer_u, peer_v, norm_final_g):
    weights = (norm_mix_g, w_in, conv_w, ret_gn_g, ret_gn_b, w_out, norm_ffn_g,
               peer_w_q, peer_sub_keys, peer_u, peer_v, norm_final_g)
    p_conv0 = jnp.zeros((DEPTH, BATCH, CONV_K - 1, CONV_WIDTH), state_conv.dtype)
    p_ret0 = jnp.zeros((DEPTH, BATCH, RET_HEADS, RET_HEAD_DIM, RET_HEAD_DIM), state_ret.dtype)
    pos_p = jnp.arange(SEQ, dtype=jnp.int32)
    y_prompt, prompt_state_conv, prompt_state_ret = trunk(x_prompt, p_conv0, p_ret0, pos_p, *weights)
    pos_s = PAST_LEN + jnp.arange(DEC_SEQ, dtype=jnp.int32)
    y_sample, sample_state_conv, sample_state_ret = trunk(x_sample, state_conv, state_ret, pos_s, *weights)
    return (y_prompt, y_sample, prompt_state_conv, prompt_state_ret, sample_state_conv, sample_state_ret)


_drawn_inputs = setup_inputs


def setup_inputs(seed=0):
    import zlib

    import numpy as np

    out = dict(_drawn_inputs(seed))
    spreads = {}
    factors = {'ret_gn_g': 11.877, 'ret_gn_b': 12.096, 'norm_final_g': 20.664, 'norm_ffn_g': 12.939}
    for name, (base, spread) in spreads.items():
        noise = np.random.default_rng([zlib.crc32(name.encode()), seed]).standard_normal(out[name].shape)
        drawn = base * np.exp(spread * noise) if base else spread * noise
        out[name] = __import__('jax').numpy.asarray(drawn.astype(out[name].dtype))
    for name, factor in factors.items():
        out[name] = (out[name] * factor).astype(out[name].dtype)
    return out
```

```python
from contextlib import ExitStack, contextmanager

import numpy as np

import concourse.bass as bass
from concourse import mybir

F32 = mybir.dt.float32
F32R = mybir.dt.float32r
U32 = mybir.dt.uint32
BF16 = mybir.dt.bfloat16
ALU = mybir.AluOpType
ACT = mybir.ActivationFunctionType
AX = mybir.AxisListType

P = 128
D = 2048
NPROMPT, NSAMPLE = 256, 8
T = NPROMPT + NSAMPLE
CH = D // P
HEADS = 8
HD = 128
PAST = 2048
NK, TOPK = 128, 16
SETS = 2 * HEADS
PICKS = HEADS * TOPK
EPS, GN_EPS = 1e-6, 1e-5

HALF = 8
HCOLS = HALF * P
RING = 4
BANKS = 4

GROUP = 8
GROUPS = NK // GROUP
QUARTER = 32
GQ = QUARTER // GROUP
QUARTERS = NK // QUARTER
GB = 11
BATCHES = T // GB
BSLOTS = (1, 4, 6, 9, 12, 14)
PARTS = 3
assert BATCHES == GQ * len(BSLOTS)

T_HEADS, T_CONV, T_OUT, T_Q = 4 * HEADS, 3 * HEADS, CH, SETS
W_CONV = T_HEADS
W_OUT = W_CONV + T_CONV
W_Q = W_OUT + T_OUT
W_U0 = W_Q + T_Q
W_MAIN = W_U0 + GROUP
TILES_ROUND = 2 * GROUP
TILES = W_MAIN + (GROUPS - 1) * TILES_ROUND + GROUP
OUTS_ROUND = GROUP + CH
FREED_U0 = (T_HEADS + T_CONV) // BANKS
FREED_MAIN = FREED_U0 + GROUP // BANKS
CONST_LOADS = 8

RECTS = ((0, 1, 16), (1, 3, 8), (4, 4, 3), (8, 8, 1))
NCAND = sum(na * nb for _, na, nb in RECTS)
ROW_LENGTHS = [nb for _, na, nb in RECTS for _ in range(na)]
ROW_STARTS = [sum(ROW_LENGTHS[:a]) for a in range(TOPK)]

TOK = ((0, 128), (128, 128), (256, 8))
ROWS = ((P, slice(0, 2)), (NSAMPLE, slice(2, 3)))

CHUNK_ORDER = [HEADS * part + h for h in range(HEADS) for part in (5, 4, 3, 6)] + \
              [HEADS * part + j for j in range(HEADS) for part in (2, 1, 0)]

CONSTS = {}


def layout_consts():
    at = 0
    for name, n in (("ones", P), ("ident", P), ("iota", P), ("cosq", T), ("sinq", T), ("cosk", T), ("sink", T),
                    ("decay", HEADS * P), ("xi", HEADS * P), ("zeta", HEADS), ("gchunk", HEADS),
                    ("gone", HEADS), ("diag", NSAMPLE), ("rows", 2 * TOPK)):
        CONSTS[name] = (at, n)
        at += n
    return at


NCONST = layout_consts()
KEEP = CONSTS["cosq"][0]


def shape_constants():
    f = np.float32
    c = np.zeros((P, NCONST), f)

    def put(name, v):
        at, n = CONSTS[name]
        c[:, at:at + n] = np.broadcast_to(np.asarray(v, f), (P, n))

    put("ones", 1.0)
    put("ident", np.eye(P))
    put("iota", np.arange(P))
    half = HD // 2
    inv = (f(10000.0) ** (-np.arange(half, dtype=f) / f(half))).astype(f)
    pos = np.concatenate([np.arange(NPROMPT), np.full(NSAMPLE, PAST)]).astype(f)
    ang = (pos[None, :] * inv[:, None]).astype(f).astype(np.float64)
    cos, sin = np.cos(ang), np.sin(ang)
    cos2, sin2 = np.concatenate([cos, cos]), np.concatenate([-sin, sin])
    put("cosq", cos2)
    put("sinq", sin2)
    put("cosk", cos2 * HD ** -0.5)
    put("sink", sin2 * HD ** -0.5)
    log_g = np.log(1.0 - 2.0 ** (-5.0 - np.arange(HEADS)))
    i = np.arange(P)
    diff = i[None, :] - i[:, None]
    decay = np.where(diff[None] >= 0, np.exp(np.maximum(diff, 0)[None] * log_g[:, None, None]), 0.0)
    put("decay", decay.transpose(1, 0, 2).reshape(P, -1))
    put("xi", np.exp((i[None, :] + 1.0) * log_g[:, None]).reshape(1, -1))
    put("zeta", np.exp((P - 1.0 - i[:, None]) * log_g[None, :]))
    put("gchunk", np.exp(P * log_g)[None])
    put("gone", np.exp(log_g)[None])
    put("diag", np.eye(P)[:, :NSAMPLE])
    put("rows", ROW_STARTS + [0] + ROW_LENGTHS[:-1])
    return c


class Chain:

    def __init__(self, eng, sem):
        self.eng, self.sem, self.base, self.k = eng, sem, 0, 0

    def did(self, ins):
        ins.then_inc(self.sem, 1)
        self.k += 1

    def wait(self):
        self.eng.wait_ge(self.sem, self.base + self.k)

    @contextmanager
    def fori(self, lo, hi, per):
        base, k = self.base, self.k
        with self.eng.Fori(lo, hi) as i:
            self.base, self.k = base + k + (i - lo) * per, 0
            yield i
            assert self.k == per, f"{self.k} chained instructions in the loop's body, not {per}"
        self.base, self.k = base, k + (hi - lo) * per


def build(nc, halves, xT, conv_state, ret_state, norm_mix, conv_w, gn_g, gn_b, norm_ffn, keysT, norm_fin,
          consts, out_yT, out_conv, out_pret, out_sret):
    with ExitStack() as ctx:
        def sb(name, shape, dt=F32, scope=ctx):
            return scope.enter_context(nc.sbuf_tensor(name, shape, dt))

        def sem(name):
            return ctx.enter_context(nc.semaphore(name))

        raw = sb("raw", [P, RING, HALF, P])
        whi = sb("whi", [P, RING, HALF, P], F32R)
        wlo = sb("wlo", [P, RING, HALF, P], F32R)
        xhi = sb("xhi", [P, CH, T], F32R)
        xlo = sb("xlo", [P, CH, T], F32R)
        acc = sb("acc", [P, CH, T])
        keep = sb("keep", [P, KEEP])
        gains = sb("gains", [P, 3, CH])
        stats = sb("stats", [P, 3, T])
        meansq, rstd, newton = stats[:, 0], stats[:, 1], stats[:, 2]
        i1T = sb("i1T", [P, T, 2], BF16)
        i2T = sb("i2T", [P, T, 2], BF16)
        gate_parts = stats[:].rearrange("p a t -> p (a t)").bitcast(BF16)\
            .rearrange("p (n t d) -> p n t d", n=PARTS, d=2)
        iota16 = sb("iota16", [P, NK], BF16)
        pair = sb("pair", [P, 2, T])

        mix = ExitStack()
        yhi = sb("yhi", [P, 2 * HEADS, T], F32R, mix)
        ylo = sb("ylo", [P, 2 * HEADS, T], F32R, mix)
        tables = sb("tables", [P, NCONST - KEEP], F32, mix)
        vT = sb("vT", [P, T], F32, mix)
        kT = sb("kT", [P, T], F32, mix)
        qT = sb("qT", [P, T], F32, mix)
        swapped = sb("swapped", [P, T], F32, mix)
        rot = sb("rot", [P, T], F32, mix)
        v_tok = sb("v_tok", [P, 2, P], F32, mix)
        k_tok = sb("k_tok", [P, 2, P], F32, mix)
        vs_tok = sb("vs_tok", [NSAMPLE, P], F32, mix)
        ks_tok = sb("ks_tok", [NSAMPLE, P], F32, mix)
        v_diag = sb("v_diag", [NSAMPLE, NSAMPLE, P], F32, mix)
        scored = sb("scored", [P, 2, P], F32, mix)
        qx = sb("qx", [P, P], F32, mix)
        state1 = sb("state1", [P, P], F32, mix)
        state2 = sb("state2", [P, P], F32, mix)
        s_old = sb("s_old", [P, NSAMPLE, P], F32, mix)
        s_new = sb("s_new", [P, NSAMPLE, P], F32, mix)
        oT = sb("oT", [P, T], F32, mix)
        dev = sb("dev", [P, T], F32, mix)
        gnorm = sb("gnorm", [P, T], F32, mix)
        silu = sb("silu", [P, T], F32, mix)
        gn = sb("gn", [P, 2, HEADS], F32, mix)
        cw = sb("cw", [P, HEADS, 3], F32, mix)
        hcs = sb("hcs", [P, T], F32, mix)
        up = sb("up", [P, 2 + NPROMPT], F32, mix)
        us = sb("us", [P, 3, NSAMPLE], F32, mix)
        sconv = sb("sconv", [P, HEADS, 2, NSAMPLE], F32, mix)
        conv_out = sb("conv_out", [P, HEADS, 2 + 2 * NSAMPLE], F32, mix)
        yv = sb("yv", [P, T], F32, mix)
        mix.close()

        gates = sb("gates", [P, 2, QUARTER, T])
        gel = sb("gel", [P, GROUP, T])
        wexp_hi = sb("wexp_hi", [P, GROUP, T], F32R)
        wexp_lo = sb("wexp_lo", [P, GROUP, T], F32R)
        onehot1 = sb("onehot1", [P, GB, QUARTER], BF16)
        gated1 = sb("gated1", [P, 2, PARTS, GB, QUARTER], BF16)
        onehot2 = sb("onehot2", [P, 2, GB, P], BF16)

        def carver(region):
            at = [0]

            def carve(*shape):
                n = int(np.prod(shape))
                at[0] += n
                assert at[0] <= QUARTER * T
                names = " ".join("abcd"[:len(shape)])
                return region[:, at[0] - n:at[0]].rearrange(f"p ({names}) -> p {names}",
                                                            **dict(zip("abcd", shape)))
            return carve

        carve = carver(gates[:, 1].rearrange("p a t -> p (a t)"))
        keys_sb = carve(SETS, NK)
        qs = carve(2, T)
        sc = carve(2, 2, NK)
        sc2 = carve(2, NK)
        best4 = carve(2, 4, TOPK)
        idx4 = carve(2, 4, TOPK).bitcast(U32)
        sval = carve(2, HEADS, 2, TOPK)
        sidx = carve(2, HEADS, 2, TOPK)
        cand1 = carve(2, NCAND)
        cand2 = carve(2, NCAND)
        pval = carve(2, TOPK)
        ppos = carve(2, TOPK).bitcast(U32)
        idle = carve(1)
        rows_sb = carve(2, TOPK)
        samp = carve(HEADS, 2, NK)
        packed = carve(2, NK)
        packed2 = carve(2, NK)
        pshift = carve(3, HEADS, TOPK)
        pexp = carve(3, HEADS, TOPK)
        carve = carver(gates[:, 0].rearrange("p a t -> p (a t)"))
        cand = carve(2, HEADS, NCAND)
        places = carve(2, HEADS, TOPK)
        rows16 = carve(TOPK).bitcast(BF16).rearrange("p (n a) -> p n a", n=2)
        marks = carve(SETS * TOPK * TOPK // 2).bitcast(BF16)
        marked = carve(SETS * TOPK * TOPK // 2).bitcast(BF16)
        twin = carve(SETS * TOPK).bitcast(BF16).rearrange("p (m d) -> p m d", d=2)
        row_of = carve(SETS, TOPK)
        keys1 = carve(SETS * TOPK // 2).bitcast(BF16)
        keys2 = carve(SETS * TOPK // 2).bitcast(BF16)
        pkval = carve(2, TOPK)
        pkidx = carve(2, TOPK).bitcast(U32)
        pkids = carve(2, 1, TOPK)
        pkcand = carve(NCAND)
        pkcand2 = carve(NCAND)
        pkpicks = carve(3, TOPK)
        pkbest = pkpicks[:, 0]
        pkpos = carve(TOPK).bitcast(U32)
        pkplaces = carve(1, TOPK)
        picks = carve(3, 3, HEADS, TOPK)
        pickv, pick1, pick2 = (picks[:, n] for n in range(3))
        pgate = carve(3, HEADS, TOPK)
        ptotal = carve(3, HEADS)
        precip = carve(3, HEADS)
        gate_rest = carve(1, T)

        bank = [ctx.enter_context(nc.psum_tensor(f"bank{b}", [P, 512], F32)) for b in range(8)]

        ones, ident, iota = (keep[:, CONSTS[n][0]:sum(CONSTS[n])] for n in ("ones", "ident", "iota"))

        def table(name):
            a, n = CONSTS[name]
            return tables[:, a - KEEP:a - KEEP + n]

        raw_full = [sem(f"raw_full{s}") for s in range(RING)]
        hi_done = sem("hi_done")
        lo_done = sem("lo_done")
        half_used = sem("half_used")
        bank_free = [sem(f"bank_free{b}") for b in range(BANKS)]
        keep_in = sem("keep_in")
        consts_in = sem("consts_in")
        x_in = [sem(f"x_in{c}") for c in range(4)]
        keys_in = sem("keys_in")
        sq_ready = sem("sq_ready")
        sq_used = sem("sq_used")
        ms_ready = sem("ms_ready")
        root_ready = sem("root_ready")
        norm_ready = sem("norm_ready")
        swap_ready = sem("swap_ready")
        rot_ready = sem("rot_ready")
        turned = sem("turned")
        tok_ready = sem("tok_ready")
        att_ready = sem("att_ready")
        st_done = sem("st_done")
        s1_ready = sem("s1_ready")
        snew_ready = sem("snew_ready")
        st_stored = sem("st_stored")
        s_in = sem("s_in")
        o_done = sem("o_done")
        o_ready = sem("o_ready")
        mean_done = sem("mean_done")
        dev_ready = sem("dev_ready")
        dsq_ready = sem("dsq_ready")
        var_done = sem("var_done")
        y_ready = sem("y_ready")
        x1_ready = sem("x1_ready")
        q_ready = sem("q_ready")
        sc_done = sem("sc_done")
        sc_ready = sem("sc_ready")
        top_done = sem("top_done")
        packed_in = sem("packed_in")
        packed_done = sem("packed_done")
        unpacked_in = sem("unpacked_in")
        gate_shift = sem("gate_shift")
        gate_exp = sem("gate_exp")
        picks_ready = sem("picks_ready")
        picks_turned = sem("picks_turned")
        gb_ready = sem("gb_ready")
        gb_used = sem("gb_used")
        gb_out = sem("gb_out")
        w_ready = sem("w_ready")
        y_out = sem("y_out")
        stored = sem("stored")
        conv_stored = sem("conv_stored")
        dve_step = sem("dve_step")

        block = ctx.enter_context(nc.Block())

        def steps_of(h):
            if not isinstance(h, int):
                return True, True, True
            return h < HEADS, 1 <= h <= HEADS, h >= 2

        def tokens_of(b):
            return bass.ds(b * GB, GB)

        @block.sync
        def _(sp):
            sp.dma_start(keep[:], consts[:, 0:KEEP]).then_inc(keep_in, 16)
            for c in range(4):
                sp.dma_start(acc[:, 4 * c:4 * c + 4, :], xT[:, 4 * c:4 * c + 4, :]).then_inc(x_in[c], 16)
            for s in range(RING):
                sp.dma_start(raw[:, s], halves[s]).then_inc(raw_full[s], 16)
            with sp.Fori(1, 2 * TILES // RING) as r:
                for s in range(RING):
                    sp.wait_ge(lo_done, r * RING + s - (RING - 1))
                    sp.dma_start(raw[:, s], halves[r * RING + s]).then_inc(raw_full[s], 16)
            for c in range(4):
                sp.wait_ge(y_out, c + 1)
                sp.dma_start(out_yT[:, 4 * c:4 * c + 4, :], acc[:, 4 * c:4 * c + 4, :]).then_inc(stored, 16)
            sp.wait_ge(stored, 4 * 16)
            sp.wait_ge(conv_stored, 16)
            sp.wait_ge(st_stored, 32 * HEADS)

        @block.gpsimd
        def _(pool):
            pool.dma_start(tables[:], consts[:, KEEP:NCONST]).then_inc(consts_in, 16)
            for i, g in enumerate((norm_mix, norm_ffn, norm_fin)):
                pool.dma_start(gains[:, i, :], g).then_inc(consts_in, 16)
            pool.dma_start(gn[:, 0, :], gn_g).then_inc(consts_in, 16)
            pool.dma_start(gn[:, 1, :], gn_b).then_inc(consts_in, 16)
            pool.dma_start(cw[:], conv_w).then_inc(consts_in, 16)
            pool.dma_start(sconv[:], conv_state).then_inc(consts_in, 16)
            sret = ret_state.rearrange("b h d e -> h d b e")
            sret_out = out_sret.rearrange("b h d e -> h d b e")
            pool.dma_start(s_old[:], sret[0]).then_inc(s_in, 16)

            def head(h, last):
                pool.wait_ge(snew_ready, h + 1)
                pool.dma_start(out_pret[h], state2[:]).then_inc(st_stored, 16)
                pool.dma_start(sret_out[h], s_new[:]).then_inc(st_stored, 16)
                if not last:
                    pool.dma_start(s_old[:], sret[h + 1]).then_inc(s_in, 16)

            with pool.Fori(0, HEADS - 1) as h:
                head(h, False)
            head(HEADS - 1, True)
            pool.wait_ge(y_ready, 2 * HEADS)
            pool.dma_start(out_conv, conv_out[:]).then_inc(conv_stored, 16)
            pool.wait_ge(conv_stored, 16)
            pool.wait_ge(st_stored, 32 * HEADS)
            pool.dma_start(keys_sb, keysT).then_inc(keys_in, 16)
            at, n = CONSTS["rows"]
            pool.dma_start(rows_sb.rearrange("p n a -> p (n a)"), consts[:, at:at + n]).then_inc(keys_in, 16)
            pool.wait_ge(sc_ready, SETS)
            for h in range(HEADS):
                pool.dma_start(packed[h * NSAMPLE:(h + 1) * NSAMPLE], samp[0:NSAMPLE, h]).then_inc(packed_in, 16)
            pool.wait_ge(packed_done, 1)
            for h in range(HEADS):
                rows = slice(h * NSAMPLE, (h + 1) * NSAMPLE)
                pool.dma_start(picks[0:NSAMPLE, :, 2, h], pkpicks[rows]).then_inc(unpacked_in, 16)

        @block.scalar
        def _(act):
            def hi_half(r, off):
                s = off % RING
                act.wait_ge(raw_full[s], 16 * (r + off // RING + 1))
                if not (isinstance(r, int) and RING * r + off < RING):
                    act.wait_ge(half_used, RING * r + off - (RING - 1))
                nc.scalar.copy(whi[:, s], raw[:, s]).then_inc(hi_done, 1)

            def ahead(r, k):
                hi_half(r, 2 * k + 2)
                hi_half(r, 2 * k + 3)

            def tile_done(r, k):
                act.wait_ge(half_used, RING * r + 2 * k + 2)

            def squares_of(c, n, src):
                if not (isinstance(n, int) and n < 2):
                    act.wait_ge(sq_used, n - 1)
                nc.scalar.activation(pair[:, c % 2], src, ACT.Square).then_inc(sq_ready, 1)

            def root(n):
                act.wait_ge(ms_ready, n)
                nc.scalar.activation(rstd, meansq, ACT.Sqrt).then_inc(root_ready, 1)

            def swap(k):
                nc.scalar.copy(swapped[0:64], bank[k][64:128, 0:T])
                nc.scalar.copy(swapped[64:128], bank[k][0:64, 0:T]).then_inc(swap_ready, 1)

            hi_half(0, 0)
            hi_half(0, 1)
            for c in range(CH):
                if c % 4 == 0:
                    act.wait_ge(x_in[c // 4], 16)
                squares_of(c, c, acc[:, c, :])
            root(1)

            def head(h):
                r, first = h * 2, isinstance(h, int) and h == 0
                tiles, att, norm = steps_of(h)
                if tiles:
                    ahead(r, 0)
                if att:
                    act.wait_ge(turned, h)
                    nc.scalar.copy(v_tok[:], bank[4][:, 0:2 * P].rearrange("p (c e) -> p c e", c=2))
                    nc.scalar.copy(vs_tok[:], bank[4][0:NSAMPLE, 2 * P:3 * P]).then_inc(tok_ready, 1)
                if norm:
                    root(h)
                if tiles:
                    tile_done(r, 0)
                    nc.scalar.copy(vT[:], bank[0][:, 0:T]).then_inc(bank_free[0], 1)
                    ahead(r, 1)
                if att:
                    act.wait_ge(st_done, h)
                    nc.scalar.copy(state1[:], bank[7][:, 0:P]).then_inc(s1_ready, 1)
                if tiles:
                    tile_done(r, 1)
                    if not first:
                        act.wait_ge(rot_ready, h * 2)
                    swap(1)
                    ahead(r, 2)
                if att:
                    act.wait_ge(o_done, h)
                    nc.scalar.copy(oT[:], bank[6][:, 0:T]).then_inc(o_ready, 1)
                    if norm:
                        act.wait_ge(y_ready, h - 1)
                    nc.scalar.activation(silu[:], bank[3][:, 0:T], ACT.Silu).then_inc(bank_free[3], 1)
                if tiles:
                    tile_done(r, 2)
                    act.wait_ge(rot_ready, h * 2 + 1)
                    swap(2)
                    ahead(r, 3)
                if att:
                    act.wait_ge(dev_ready, h)
                    nc.scalar.activation(gnorm[:], dev[:], ACT.Square).then_inc(dsq_ready, 1)

            for h in range(2):
                head(h)
            with act.Fori(2, HEADS) as h:
                head(h)
            for h in range(HEADS, HEADS + 2):
                head(h)

            r0 = W_CONV // 2
            with act.Fori(0, HEADS // 4) as i:
                for j in range(4):
                    for n in range(3):
                        k = 3 * j + n
                        ahead(r0 + i * 6, k)
                        if n == 0:
                            tile_done(r0 + i * 6, k)
                            act.wait_ge(y_ready, HEADS + i * 4 + j)
                            nc.scalar.copy(hcs[:], bank[k % BANKS][:, 0:T]).then_inc(bank_free[k % BANKS], 1)

            r0 = W_OUT // 2
            with act.Fori(0, CH // 4) as i:
                for k in range(4):
                    ahead(r0 + i * 2, k)
                    act.wait_ge(x1_ready, i * 4 + k + 1)
                    squares_of(k, CH + i * 4 + k, acc[:, i * 4 + k, :])

            root(HEADS + 2)

            samp_sets = samp.rearrange("p h c k -> p (h c) k")

            def scores_out(j, b):
                act.wait_ge(sc_done, j + 1)
                if not isinstance(j, int) or j >= 2:
                    act.wait_ge(top_done, j - 1)
                nc.scalar.copy(sc[:, b, 0:2], bank[4 + b][:, 0:2 * NK].rearrange("p (t k) -> p t k", t=2))
                nc.scalar.copy(samp_sets[0:NSAMPLE, bass.ds(j, 1)],
                               bank[4 + b][0:NSAMPLE, 2 * NK:3 * NK].unsqueeze(1)).then_inc(sc_ready, 1)

            r0 = W_Q // 2

            act.wait_ge(keys_in, 32)

            def query_tiles(i):
                for k in range(4):
                    ahead(r0 + i * 2, k)
                    tile_done(r0 + i * 2, k)
                    first = isinstance(i, int) and i == 0
                    if not (first and k < 2):
                        act.wait_ge(sc_done, i * 4 + k - 1)
                    nc.scalar.copy(qs[:, k % 2], bank[k][:, 0:T]).then_inc(q_ready, 1)
                    if not (first and k == 0):
                        scores_out(i * 4 + k - 1, (k - 1) % 2)

            query_tiles(0)
            with act.Fori(1, SETS // 4) as i:
                query_tiles(i)
            scores_out(SETS - 1, (SETS - 1) % 2)

            def gelu_out(r, k, w_need):
                tile_done(r, k)
                if w_need is not None:
                    act.wait_ge(w_ready, w_need)
                b = k % BANKS
                nc.scalar.activation(gel[:, k], bank[b][:, 0:T], ACT.Gelu).then_inc(bank_free[b], 1)

            for k in range(GROUP):
                ahead(W_U0 // 2, k)
                gelu_out(W_U0 // 2, k, None)

            act.wait_ge(gate_shift, 1)
            nc.scalar.activation(pexp[:, 0:2], pshift[:, 0:2], ACT.Exp)
            nc.scalar.activation(pexp[0:NSAMPLE, 2], pshift[0:NSAMPLE, 2], ACT.Exp).then_inc(gate_exp, 1)

            def batch_out(q, n, b, even):
                act.wait_ge(gb_used, n + 1)
                src = bank[4 + even][:, 0:GB * QUARTER].rearrange("p (t a) -> p a t", t=GB)
                nc.scalar.copy(gates[:, q % 2, :, tokens_of(b)], src).then_inc(gb_out, 1)

            with act.Fori(0, BATCHES // 2) as i:
                for e in range(2):
                    batch_out(0, i * 2 + e, i * 2 + e, e)

            def rounds(q, g, rr, build):
                r = W_MAIN // 2 + g * (TILES_ROUND // 2)
                for k in range(TILES_ROUND):
                    ahead(r, k)
                    if 0 < k <= GROUP:
                        gelu_out(r, k - 1, g * GROUP + k)
                    if build and k - 1 in BSLOTS:
                        slot = BSLOTS.index(k - 1)
                        b = rr * len(BSLOTS) + slot
                        batch_out(q + 1, (q + 1) * BATCHES + b, b, slot % 2)

            with act.Fori(0, QUARTERS - 1) as q:
                with act.Fori(0, GQ) as rr:
                    rounds(q, q * GQ + rr, rr, True)
            with act.Fori(0, GQ - 1) as rr:
                rounds(QUARTERS - 1, (QUARTERS - 1) * GQ + rr, rr, False)
            r = W_MAIN // 2 + (GROUPS - 1) * (TILES_ROUND // 2)
            for c in range(CH):
                if c % 2 == 0 and c // 2 < GROUP - 1:
                    ahead(r, c // 2)
                act.wait_ge(bank_free[c % BANKS],
                            FREED_MAIN + (GROUPS - 1) * (OUTS_ROUND // BANKS) + c // BANKS + 1)
                squares_of(c, 2 * CH + c, acc[:, c, :])
            root(HEADS + 3)

        @block.tensor
        def _(pe):
            def half(r, off, out, mh, ml, start, stop, waits=()):
                s = off % RING
                pe.wait_ge(lo_done, RING * r + off + 1)
                for c in range(HALF):
                    for sem_, need in (waits[c] if c in waits else ()):
                        pe.wait_ge(sem_, need)
                    nc.tensor.matmul(out, whi[:, s, c], mh[c], start=start and c == 0, stop=False)
                    nc.tensor.matmul(out, whi[:, s, c], ml[c], start=False, stop=False)
                    mm = nc.tensor.matmul(out, wlo[:, s, c], mh[c], start=False, stop=stop and c == HALF - 1)
                mm.then_inc(half_used, 1)

            def out_free(o4, off):
                if o4 is None or isinstance(o4, int) and BANKS * o4 + off < BANKS:
                    return
                pe.wait_ge(bank_free[off % BANKS], o4 + off // BANKS)

            def tile(r, k, o4, off, hi_, lo_, waits=({}, {}), between=None):
                out_free(o4, off)
                b = bank[off % BANKS][:, 0:T]
                half(r, 2 * k, b, [hi_[:, c, :] for c in range(HALF)], [lo_[:, c, :] for c in range(HALF)],
                     True, False, waits[0])
                if between:
                    between()
                half(r, 2 * k + 1, b, [hi_[:, HALF + c, :] for c in range(HALF)],
                     [lo_[:, HALF + c, :] for c in range(HALF)], False, True, waits[1])

            def add_squares(c, n):
                pe.wait_ge(sq_ready, n + 1)
                nc.tensor.matmul(bank[7][:, 0:T], ones, pair[:, c % 2], start=c == 0, stop=c == CH - 1)\
                    .then_inc(sq_used, 1)

            def norm_waits(base):
                return tuple({c: [(norm_ready, base + (s * HALF + c) // 2 + 1)] for c in range(0, HALF, 2)}
                             for s in range(2))

            pe.wait_ge(keep_in, 16)
            for c in range(CH):
                add_squares(c, c)

            def turn(p):
                pe.wait_ge(bank_free[0], p + 1)
                pe.wait_ge(rot_ready, 2 * p + 2)
                for t in range(2):
                    nc.tensor.transpose(bank[4][:, t * P:(t + 1) * P], vT[:, t * P:(t + 1) * P], ident)
                nc.tensor.transpose(bank[4][0:NSAMPLE, 2 * P:3 * P], vT[:, NPROMPT:T], ident)
                for t in range(2):
                    nc.tensor.transpose(bank[5][:, t * P:(t + 1) * P], kT[:, t * P:(t + 1) * P], ident)
                nc.tensor.transpose(bank[5][0:NSAMPLE, 2 * P:3 * P], kT[:, NPROMPT:T], ident)
                for t in range(2):
                    mm = nc.tensor.matmul(bank[6][:, t * P:(t + 1) * P], kT[:, t * P:(t + 1) * P],
                                          qT[:, t * P:(t + 1) * P], start=True, stop=True)
                mm.then_inc(turned, 1)

            def states(p):
                if not (isinstance(p, int) and p == 0):
                    pe.wait_ge(ms_ready, p + 1)
                pe.wait_ge(tok_ready, p + 1)
                pe.wait_ge(att_ready, p + 1)
                for t in range(2):
                    nc.tensor.matmul(bank[7][:, t * P:(t + 1) * P], k_tok[:, t], v_tok[:, t], start=True, stop=True)
                for t in range(2):
                    mm = nc.tensor.matmul(bank[4 + t][:], ks_tok[:], v_diag[:, 4 * t:4 * t + 4, :],
                                          start=True, stop=True)
                mm.then_inc(st_done, 1)

            def outputs(p):
                pe.wait_ge(s1_ready, p + 1)
                nc.tensor.matmul(bank[6][:, 0:P], v_tok[:, 0], scored[:, 0], start=True, stop=True)
                nc.tensor.matmul(bank[6][:, P:2 * P], v_tok[:, 1], scored[:, 1], start=True, stop=False)
                nc.tensor.matmul(bank[6][:, P:2 * P], state1[:], qx[:], start=False, stop=True)
                pe.wait_ge(snew_ready, p + 1)
                for b in range(NSAMPLE):
                    mm = nc.tensor.matmul(bank[6][:, NPROMPT + b:NPROMPT + b + 1], s_new[:, b],
                                          qT[:, NPROMPT + b:NPROMPT + b + 1], start=True, stop=True)
                mm.then_inc(o_done, 1)

            def mean(p):
                pe.wait_ge(o_ready, p + 1)
                nc.tensor.matmul(bank[7][:, 0:T], ones, oT[:], start=True, stop=True).then_inc(mean_done, 1)

            def variance(p):
                pe.wait_ge(dsq_ready, p + 1)
                nc.tensor.matmul(bank[7][:, 0:T], ones, gnorm[:], start=True, stop=True).then_inc(var_done, 1)

            def head(h):
                r, first = h * 2, isinstance(h, int) and h == 0
                tiles, att, _ = steps_of(h)
                for k, part in enumerate((turn, states, outputs, mean)):
                    if att:
                        part(h - 1)
                    if tiles:
                        tile(r, k, h, k, xhi, xlo, norm_waits(0) if first and k == 0 else ({}, {}))
                if att:
                    variance(h - 1)

            for h in range(2):
                head(h)
            with pe.Fori(2, HEADS) as h:
                head(h)
            head(HEADS)

            with pe.Fori(0, HEADS // 4) as i:
                for k in range(12):
                    tile(W_CONV // 2 + i * 6, k, W_CONV // BANKS + i * 3, k, xhi, xlo)

            def out_tiles(i):
                first = isinstance(i, int) and i == 0
                for k in range(4):
                    w = ({}, {})
                    if first and k == 0:
                        w = tuple({c: [(y_ready, s * HALF + c + 1)] for c in range(HALF)} for s in range(2))
                    between = None
                    if not (first and k == 0):
                        def between(k=k):
                            n = CH + i * 4 + k - 1
                            pe.wait_ge(sq_ready, n + 1)
                            nc.tensor.matmul(bank[7][:, 0:T], ones, pair[:, (k - 1) % 2],
                                             start=first and k == 1, stop=False).then_inc(sq_used, 1)
                    if not first:
                        pe.wait_ge(x1_ready, i * 4 + k - 3)
                    tile(W_OUT // 2 + i * 2, k, FREED_U0 if first else None, k, yhi, ylo, w, between)

            out_tiles(0)
            with pe.Fori(1, CH // 4) as i:
                out_tiles(i)
            pe.wait_ge(sq_ready, 2 * CH)
            nc.tensor.matmul(bank[7][:, 0:T], ones, pair[:, 1], start=False, stop=True).then_inc(sq_used, 1)

            def score(j, b):
                pe.wait_ge(q_ready, j + 1)
                if not isinstance(j, int) or j >= 2:
                    pe.wait_ge(sc_ready, j - 1)
                for t, (t0, n) in enumerate(TOK):
                    mm = nc.tensor.matmul(bank[4 + b][0:n, t * NK:(t + 1) * NK], qs[:, b, t0:t0 + n],
                                          keys_sb[:, j, :], start=True, stop=True)
                mm.then_inc(sc_done, 1)

            def query_tiles(i):
                first = isinstance(i, int) and i == 0
                for k in range(4):
                    w = norm_waits(CH // 2) if first and k == 0 else ({}, {})
                    if first:
                        pe.wait_ge(x1_ready, CH - BANKS + k + 1)
                    else:
                        pe.wait_ge(q_ready, i * 4 + k - 3)
                    b = bank[k][:, 0:T]
                    r = W_Q // 2 + i * 2
                    half(r, 2 * k, b, [xhi[:, c, :] for c in range(HALF)], [xlo[:, c, :] for c in range(HALF)],
                         True, False, w[0])
                    if not (first and k == 0):
                        if first and k == 1:
                            pe.wait_ge(keys_in, 32)
                        score(i * 4 + k - 1, (k - 1) % 2)
                    half(r, 2 * k + 1, b, [xhi[:, HALF + c, :] for c in range(HALF)],
                         [xlo[:, HALF + c, :] for c in range(HALF)], False, True, w[1])

            query_tiles(0)
            with pe.Fori(1, SETS // 4) as i:
                query_tiles(i)
            score(SETS - 1, (SETS - 1) % 2)

            for k in range(GROUP):
                if k < BANKS:
                    pe.wait_ge(q_ready, SETS - BANKS + k + 1)
                    b = bank[k][:, 0:T]
                    for s in range(2):
                        half(W_U0 // 2, 2 * k + s, b, [xhi[:, s * HALF + c, :] for c in range(HALF)],
                             [xlo[:, s * HALF + c, :] for c in range(HALF)], s == 0, s == 1)
                else:
                    tile(W_U0 // 2, k, FREED_U0, k, xhi, xlo)

            pe.wait_ge(picks_ready, 1)
            for b, src in ((4, pick1), (5, pick2), (6, pgate)):
                for t, (t0, n) in enumerate(TOK):
                    flat = src[:, t].rearrange("p h k -> p (h k)")
                    mm = nc.tensor.transpose(bank[b][:, t0:t0 + n], flat[0:n], ident[0:n, 0:n])
            mm.then_inc(picks_turned, 1)

            def batch(n, e):
                pe.wait_ge(gb_ready, n + 1)
                if not (isinstance(n, int) and n < 2):
                    pe.wait_ge(gb_out, n - 1)
                for t in range(GB):
                    o = bank[4 + e][:, t * QUARTER:(t + 1) * QUARTER]
                    for part in range(PARTS):
                        mm = nc.tensor.matmul(o, onehot2[:, e, t], gated1[:, e, part, t],
                                              start=part == 0, stop=part == PARTS - 1)
                mm.then_inc(gb_used, 1)

            for n in range(2):
                batch(n, n)
            with pe.Fori(1, BATCHES // 2) as i:
                for e in range(2):
                    batch(i * 2 + e, e)

            def v_tiles(r, k0, o4, off0, g, hook):
                for k in range(GROUP):
                    for s in range(2):
                        off = off0 + 2 * k + s
                        out_free(o4, off)
                        w = {0: [(w_ready, (g + 1) * GROUP)]} if k == 0 and s == 0 else {}
                        half(r, 2 * (k0 + k) + s, bank[off % BANKS][:, 0:T], [wexp_hi[:, c] for c in range(GROUP)],
                             [wexp_lo[:, c] for c in range(GROUP)], True, True, w)
                    hook(k0 + k)

            def rounds(q, g, rr, build):
                r = W_MAIN // 2 + g * (TILES_ROUND // 2)
                o4 = FREED_MAIN + g * (OUTS_ROUND // BANKS)

                def hook(k):
                    if build and k in BSLOTS:
                        slot = BSLOTS.index(k)
                        batch((q + 1) * BATCHES + rr * len(BSLOTS) + slot, slot % 2)

                for k in range(GROUP):
                    tile(r, k, o4, k, xhi, xlo)
                    hook(k)
                v_tiles(r, GROUP, o4, GROUP, g, hook)

            with pe.Fori(0, QUARTERS - 1) as q:
                with pe.Fori(0, GQ) as rr:
                    rounds(q, q * GQ + rr, rr, True)
            with pe.Fori(0, GQ - 1) as rr:
                rounds(QUARTERS - 1, (QUARTERS - 1) * GQ + rr, rr, False)
            g = GROUPS - 1

            def squares_before(k):
                for c in (2 * k - 2, 2 * k - 1):
                    if c >= 0:
                        add_squares(c, 2 * CH + c)

            v_tiles(W_MAIN // 2 + g * (TILES_ROUND // 2), 0, FREED_MAIN + g * (OUTS_ROUND // BANKS), 0, g,
                    squares_before)
            squares_before(GROUP)

        @block.vector
        def _(dve):
            v = nc.vector
            ch = Chain(dve, dve_step)

            def lo_half(r, off):
                s = off % RING
                dve.wait_ge(hi_done, RING * r + off + 1)
                v.tensor_tensor(wlo[:, s], raw[:, s], whi[:, s].bitcast(F32), ALU.subtract).then_inc(lo_done, 1)

            def ahead(r, k):
                lo_half(r, 2 * k + 2)
                lo_half(r, 2 * k + 3)

            def tile_done(r, k):
                dve.wait_ge(half_used, RING * r + 2 * k + 2)

            def mean_square(scale, eps, src, need):
                for s_, n_ in need:
                    dve.wait_ge(s_, n_)
                v.tensor_scalar(meansq, src, scale, eps, ALU.mult, ALU.add).then_inc(ms_ready, 1)

            def reciprocal_root(n):
                dve.wait_ge(root_ready, n)
                ch.did(v.reciprocal(rstd, rstd))
                ch.wait()
                ch.did(v.tensor_tensor(newton, rstd, rstd, ALU.mult))
                ch.wait()
                ch.did(v.tensor_tensor(newton, newton, meansq, ALU.mult))
                ch.wait()
                ch.did(v.tensor_scalar(newton, newton, -0.5, 1.5, ALU.mult, ALU.add))
                ch.wait()
                ch.did(v.tensor_tensor(rstd, rstd, newton, ALU.mult))
                ch.wait()

            def normalise(i):
                for b in range(CH // 2):
                    if i or b:
                        dve.wait_ge(norm_ready, i * (CH // 2) + b)
                    for c in range(2):
                        last = v.scalar_tensor_tensor(out=pair[:, c], in0=acc[:, 2 * b + c, :],
                                                      scalar=gains[:, i, 2 * b + c:2 * b + c + 1],
                                                      in1=rstd, op0=ALU.mult, op1=ALU.mult)
                    ch.did(last)
                    ch.wait()
                    ch.did(v.tensor_copy(xhi[:, 2 * b:2 * b + 2, :], pair[:]))
                    ch.wait()
                    v.tensor_tensor(xlo[:, 2 * b:2 * b + 2, :], pair[:], xhi[:, 2 * b:2 * b + 2, :].bitcast(F32),
                                    ALU.subtract).then_inc(norm_ready, 1)

            dve.wait_ge(consts_in, 16 * CONST_LOADS)
            for c in range(4):
                dve.wait_ge(x_in[c], 16)
            lo_half(0, 0)
            lo_half(0, 1)
            mean_square(1.0 / D, EPS, bank[7][:, 0:T], [(sq_used, CH)])
            reciprocal_root(1)
            normalise(0)

            def rotate(dst, b, cos, sin, n):
                dve.wait_ge(swap_ready, n + 1)
                if not (isinstance(n, int) and n == 0):
                    dve.wait_ge(rot_ready, n)
                v.tensor_tensor(dst[:], bank[b][:, 0:T], table(cos), ALU.mult).then_inc(bank_free[b], 1)
                ch.did(v.tensor_tensor(rot[:], swapped[:], table(sin), ALU.mult))
                ch.wait()
                v.tensor_tensor(dst[:], dst[:], rot[:], ALU.add).then_inc(rot_ready, 1)

            def of_head(name, p, n=1):
                return table(name)[:, bass.ds(p * n, n)]

            def attention_in(p):
                dve.wait_ge(turned, p + 1)
                v.tensor_scalar(k_tok[:], bank[5][:, 0:2 * P].rearrange("p (c e) -> p c e", c=2),
                                of_head("zeta", p), None, ALU.mult)
                v.tensor_copy(ks_tok[:], bank[5][0:NSAMPLE, 2 * P:3 * P])
                v.tensor_tensor(scored[:], bank[6][:, 0:2 * P].rearrange("p (c e) -> p c e", c=2),
                                of_head("decay", p, P).unsqueeze(1).to_broadcast([P, 2, P]), ALU.mult)
                v.tensor_tensor(qx[:], qT[:, P:2 * P], of_head("xi", p, P), ALU.mult)
                dve.wait_ge(tok_ready, p + 1)
                v.tensor_tensor(v_diag[:], vs_tok[:].unsqueeze(1).to_broadcast([NSAMPLE, NSAMPLE, P]),
                                table("diag")[0:NSAMPLE].unsqueeze(2).to_broadcast([NSAMPLE, NSAMPLE, P]),
                                ALU.mult).then_inc(att_ready, 1)

            def new_states(p):
                dve.wait_ge(st_done, p + 1)
                dve.wait_ge(s1_ready, p + 1)
                if not (isinstance(p, int) and p == 0):
                    dve.wait_ge(st_stored, p * 32)
                v.scalar_tensor_tensor(out=state2[:], in0=state1[:], scalar=of_head("gchunk", p),
                                       in1=bank[7][:, P:2 * P], op0=ALU.mult, op1=ALU.add)
                dve.wait_ge(s_in, (p + 1) * 16)
                for t in range(2):
                    last = v.scalar_tensor_tensor(
                        out=s_new[:, 4 * t:4 * t + 4, :], in0=s_old[:, 4 * t:4 * t + 4, :],
                        scalar=of_head("gone", p), in1=bank[4 + t][:].rearrange("p (b e) -> p b e", b=4),
                        op0=ALU.mult, op1=ALU.add)
                last.then_inc(snew_ready, 1)

            def deviation(p):
                dve.wait_ge(o_ready, p + 1)
                dve.wait_ge(mean_done, p + 1)
                v.scalar_tensor_tensor(out=dev[:], in0=bank[7][:, 0:T], scalar=-1.0 / HD, in1=oT[:],
                                       op0=ALU.mult, op1=ALU.add).then_inc(dev_ready, 1)

            def normed(p):
                reciprocal_root(p + 2)
                if not (isinstance(p, int) and p == 0):
                    dve.wait_ge(y_ready, p)
                ch.did(v.tensor_tensor(yv[:], dev[:], rstd, ALU.mult))
                ch.wait()
                ch.did(v.tensor_scalar(yv[:], yv[:], gn[:, 0, bass.ds(p, 1)], gn[:, 1, bass.ds(p, 1)],
                                       ALU.mult, ALU.add))
                ch.wait()
                dve.wait_ge(bank_free[3], p + 1)
                ch.did(v.tensor_tensor(yv[:], yv[:], silu[:], ALU.mult))
                split_y(p)

            def head(h):
                r = h * 2
                tiles, att, norm = steps_of(h)
                if tiles:
                    ahead(r, 0)
                if norm:
                    mean_square(1.0 / HD, GN_EPS, bank[7][:, 0:T], [(var_done, h - 1)])
                if att:
                    attention_in(h - 1)
                if tiles:
                    ahead(r, 1)
                if att:
                    new_states(h - 1)
                if norm:
                    normed(h - 2)
                if tiles:
                    ahead(r, 2)
                    tile_done(r, 1)
                    rotate(kT, 1, "cosk", "sink", h * 2)
                    ahead(r, 3)
                if att:
                    dve.wait_ge(o_done, h)
                if tiles:
                    tile_done(r, 2)
                    rotate(qT, 2, "cosq", "sinq", h * 2 + 1)
                if att:
                    deviation(h - 1)

            def split_y(c):
                ch.wait()
                ch.did(v.tensor_copy(yhi[:, bass.ds(c, 1), :], yv[:].unsqueeze(1)))
                ch.wait()
                v.tensor_tensor(ylo[:, bass.ds(c, 1), :], yv[:].unsqueeze(1),
                                yhi[:, bass.ds(c, 1), :].bitcast(F32), ALU.subtract).then_inc(y_ready, 1)

            for h in range(2):
                head(h)
            with ch.fori(2, HEADS, 11) as h:
                head(h)
            for h in range(HEADS, HEADS + 2):
                head(h)

            ch.did(v.memset(up[:, 0:2], 0.0))
            with ch.fori(0, HEADS // 4, 4 * 7) as i:
                r, o4 = W_CONV // 2 + i * 6, W_CONV // BANKS + i * 3
                for j in range(4):
                    c = i * 4 + j
                    sel = bass.ds(c, 1)
                    ahead(r, 3 * j)
                    dve.wait_ge(y_ready, HEADS + c)
                    ch.did(v.tensor_copy(us[:, 0:2, :], sconv[:, sel].rearrange("p c a b -> p (c a) b")))
                    ahead(r, 3 * j + 1)
                    bh, bc, bb = ((3 * j + n) % BANKS for n in range(3))
                    tile_done(r, 3 * j + 1)
                    dve.wait_ge(bank_free[bh], o4 + (3 * j) // BANKS + 1)
                    ch.did(v.tensor_tensor(us[:, 2, :], bank[bc][:, NPROMPT:T], hcs[:, NPROMPT:T], ALU.mult))
                    v.tensor_tensor(up[:, 2:], bank[bc][:, 0:NPROMPT], hcs[:, 0:NPROMPT], ALU.mult)\
                        .then_inc(bank_free[bc], 1)
                    dve.wait_ge(bank_free[bc], o4 + (3 * j + 1) // BANKS + 1)
                    ch.wait()
                    taps = [cw[:, sel, n:n + 1].rearrange("p c n -> p (c n)") for n in range(3)]
                    v.tensor_copy(conv_out[:, sel, 0:2].rearrange("p c n -> p (c n)"), up[:, NPROMPT:])
                    ch.did(v.tensor_copy(conv_out[:, sel, 2:].rearrange("p c n -> p (c n)"),
                                         us[:, 1:3, :].rearrange("p a b -> p (a b)")))
                    v.tensor_scalar(yv[:, 0:NPROMPT], up[:, 0:NPROMPT], taps[0], None, ALU.mult)
                    ch.did(v.tensor_scalar(yv[:, NPROMPT:], us[:, 0, :], taps[0], None, ALU.mult))
                    for n in range(1, 3):
                        ch.wait()
                        v.scalar_tensor_tensor(out=yv[:, 0:NPROMPT], in0=up[:, n:n + NPROMPT], scalar=taps[n],
                                               in1=yv[:, 0:NPROMPT], op0=ALU.mult, op1=ALU.add)
                        ch.did(v.scalar_tensor_tensor(out=yv[:, NPROMPT:], in0=us[:, n, :], scalar=taps[n],
                                                      in1=yv[:, NPROMPT:], op0=ALU.mult, op1=ALU.add))
                    ahead(r, 3 * j + 2)
                    tile_done(r, 3 * j + 2)
                    ch.wait()
                    v.tensor_tensor(yv[:], yv[:], bank[bb][:, 0:T], ALU.mult).then_inc(bank_free[bb], 1)
                    dve.wait_ge(bank_free[bb], o4 + (3 * j + 2) // BANKS + 1)
                    split_y(HEADS + c)

            with dve.Fori(0, CH // 4) as i:
                for k in range(4):
                    r = W_OUT // 2 + i * 2
                    ahead(r, k)
                    tile_done(r, k)
                    c = acc[:, bass.ds(i * 4 + k, 1), :]
                    v.tensor_tensor(c, bank[k][:, 0:T].unsqueeze(1), c, ALU.add).then_inc(x1_ready, 1)

            mean_square(1.0 / D, EPS, bank[7][:, 0:T], [(sq_used, 2 * CH)])
            reciprocal_root(HEADS + 2)
            normalise(1)

            def hold():
                ch.wait()
                v.memset(idle, 0.0)

            def top16(vals, idx, src, tmp):
                every = range(len(src))
                for t in every:
                    last = v.max(vals[t][:, 0:8], src[t])
                ch.did(last)
                hold()
                for t in every:
                    v.max_index(idx[t][:, 0:8], vals[t][:, 0:8], src[t])
                    last = v.match_replace(tmp[t], vals[t][:, 0:8], src[t], -3.0e38)
                ch.did(last)
                hold()
                for t in every:
                    last = v.max(vals[t][:, 8:16], tmp[t])
                ch.did(last)
                hold()
                for t in every:
                    last = v.max_index(idx[t][:, 8:16], vals[t][:, 8:16], tmp[t])
                return last

            def top_set(j, b, k):
                dve.wait_ge(sc_ready, j + 1)
                if not (isinstance(j, int) and j == 0):
                    dve.wait_ge(top_done, j)
                ch.wait()
                v.memset(idle, 0.0)
                top16([best4[:, t, k] for t in range(2)], [idx4[:, t, k] for t in range(2)],
                      [sc[:, b, t] for t in range(2)], [sc2[:, t] for t in range(2)]).then_inc(top_done, 1)

            def keep_sets(i):
                dve.wait_ge(top_done, i * 4 + 4)
                heads = bass.ds(i * 2, 2)
                for t in range(2):
                    b4 = best4[:, t].rearrange("p (h c) k -> p h c k", c=2)
                    i4 = idx4[:, t].rearrange("p (h c) k -> p h c k", c=2)
                    v.tensor_copy(sval[:, t, heads], b4)
                    last = v.tensor_copy(sidx[:, t, heads], i4)
                ch.did(last)

            def query_tiles(i):
                for k in range(4):
                    ahead(W_Q // 2 + i * 2, k)
                    if isinstance(i, int) and k == 0:
                        continue
                    top_set(i * 4 + k - 1, (k - 1) % 2, (k - 1) % 4)
                    if k == 0:
                        keep_sets(i - 1)

            query_tiles(0)
            with ch.fori(1, SETS // 4, 4 * 3 + 1) as i:
                query_tiles(i)
            ahead(W_U0 // 2, 0)
            top_set(SETS - 1, 1, 3)
            keep_sets(SETS // 4 - 1)
            ch.wait()

            def sums(out, lists, middle):
                first, second = lists
                at = 0
                for a0, na, nb in RECTS:
                    shape = middle + [na, nb]
                    k = len(middle)
                    place = (slice(None),) * k
                    o = out[place + (slice(at, at + na * nb),)]
                    o = o.rearrange("p (a b) -> p a b", a=na) if k == 1 else o.rearrange("p h (a b) -> p h a b", a=na)
                    last = v.tensor_tensor(o, first[place + (slice(a0, a0 + na),)].unsqueeze(k + 1).to_broadcast(shape),
                                           second[place + (slice(0, nb),)].unsqueeze(k).to_broadcast(shape), ALU.add)
                    at += na * nb
                return last

            def compare(n, m, with_, op):
                shape = [n, m * TOPK, TOPK // 2, 2]
                return v.tensor_tensor(marks[0:n, 0:m * TOPK * TOPK].rearrange("p (q a d) -> p q a d", a=TOPK // 2, d=2),
                                       twin[0:n, 0:m * TOPK].unsqueeze(2).to_broadcast(shape),
                                       with_[0:n].rearrange("p (a d) -> p a d", d=2).unsqueeze(1).to_broadcast(shape),
                                       op)

            def marked_sum(out, n, m, values):
                def view(x):
                    return x[0:n, 0:m * TOPK * TOPK].rearrange("p (m k a) -> p m k a", k=TOPK, a=TOPK)

                ch.did(v.tensor_tensor(view(marked), view(marks), values.to_broadcast([n, m, TOPK, TOPK]), ALU.mult))
                ch.wait()
                ch.did(v.tensor_reduce(out, view(marked), AX.X, ALU.add))
                ch.wait()

            def decode(n, m, places, ids1, ids2, out1, out2):
                def lists(x):
                    return x[0:n, 0:m * TOPK].rearrange("p (m a) -> p m a", a=TOPK)

                def pairs(x):
                    return x.rearrange("p m k -> p (m k)").unsqueeze(2).to_broadcast([n, m * TOPK, 2])

                v.tensor_copy(lists(keys1)[:, :, 0:1], ids1[:, :, 0:1])
                v.tensor_tensor(lists(keys1)[:, :, 1:], ids1[:, :, 1:], ids1[:, :, :TOPK - 1], ALU.subtract)
                v.tensor_copy(lists(keys2), ids2)
                ch.did(v.tensor_copy(twin[0:n, 0:m * TOPK], pairs(places)))
                ch.wait()
                ch.did(compare(n, m, rows16[:, 0], ALU.is_ge))
                ch.wait()
                marked_sum(out1, n, m, lists(keys1).unsqueeze(2))
                marked_sum(row_of[0:n, 0:m], n, m, rows16[0:n, 1].unsqueeze(1).unsqueeze(1))
                ch.did(v.tensor_tensor(twin[0:n, 0:m * TOPK], pairs(places), pairs(row_of[0:n, 0:m]), ALU.subtract))
                ch.wait()
                ch.did(compare(n, m, iota16[:, 0:TOPK], ALU.is_equal))
                ch.wait()
                marked_sum(out2, n, m, lists(keys2).unsqueeze(2))

            dve.wait_ge(keys_in, 32)
            v.tensor_copy(iota16[:], iota)
            ch.did(v.tensor_copy(rows16, rows_sb))

            n = HEADS * NSAMPLE
            dve.wait_ge(packed_in, 16 * HEADS)
            last = top16([pkval[0:n, c] for c in range(2)], [pkidx[0:n, c] for c in range(2)],
                         [packed[0:n, c] for c in range(2)], [packed2[0:n, c] for c in range(2)])
            ch.did(last)
            ch.wait()
            ch.did(v.tensor_copy(pkids[0:n, :, 0], pkidx[0:n]))
            ch.did(sums(pkcand[0:n], (pkval[0:n, 0], pkval[0:n, 1]), [n]))
            hold()
            ch.did(top16([pkbest[0:n]], [pkpos[0:n]], [pkcand[0:n]], [pkcand2[0:n]]))
            ch.wait()
            ch.did(v.tensor_copy(pkplaces[0:n, 0], pkpos[0:n]))
            ch.wait()
            decode(n, 1, pkplaces[0:n], pkids[0:n, 0], pkids[0:n, 1], pkpicks[0:n, 1:2], pkpicks[0:n, 2:3])
            v.memset(idle, 0.0).then_inc(packed_done, 1)

            for t in range(2):
                last = sums(cand[:, t], (sval[:, t, :, 0], sval[:, t, :, 1]), [P, HEADS])
            ch.did(last)

            def route(i, e):
                h = bass.ds(i * 2 + e, 1)
                ch.wait()
                ch.did(v.tensor_copy(cand1.unsqueeze(2), cand[:, :, h]))
                hold()
                ch.did(top16([pval[:, t] for t in range(2)], [ppos[:, t] for t in range(2)],
                             [cand1[:, t] for t in range(2)], [cand2[:, t] for t in range(2)]))
                ch.wait()
                v.tensor_copy(pickv[:, 0:2, h], pval.unsqueeze(2))
                ch.did(v.tensor_copy(places[:, :, h], ppos.unsqueeze(2)))

            ahead(W_U0 // 2, 1)
            route(0, 0)
            route(0, 1)
            with ch.fori(1, HEADS // 2, 2 * 6) as i:
                for e in range(2):
                    ahead(W_U0 // 2 + i, e)
                    route(i, e)
            ch.wait()
            dve.wait_ge(unpacked_in, 16 * HEADS)

            for n, t in ROWS:
                nt = t.stop - t.start
                last = v.tensor_tensor(pshift[0:n, t], pickv[0:n, t],
                                       pickv[0:n, t, :, 0:1].to_broadcast([n, nt, HEADS, TOPK]), ALU.subtract)
            last.then_inc(gate_shift, 1)
            def all_heads(x):
                return x.rearrange("p t h k -> p (t h) k")

            decode(P, SETS, all_heads(places), all_heads(sidx[:, :, :, 0]), all_heads(sidx[:, :, :, 1]), all_heads(pick1[:, 0:2]), all_heads(pick2[:, 0:2]))
            dve.wait_ge(gate_exp, 1)
            for n, t in ROWS:
                last = v.tensor_reduce(ptotal[0:n, t], pexp[0:n, t], AX.X, ALU.add)
            ch.did(last)
            ch.wait()
            for n, t in ROWS:
                last = v.reciprocal(precip[0:n, t], ptotal[0:n, t])
            ch.did(last)
            ch.wait()
            for n, t in ROWS:
                nt = t.stop - t.start
                last = v.tensor_tensor(pgate[0:n, t], pexp[0:n, t],
                                       precip[0:n, t].unsqueeze(3).to_broadcast([n, nt, HEADS, TOPK]), ALU.mult)
            last.then_inc(picks_ready, 1)
            dve.wait_ge(picks_turned, 1)
            def twice(x):
                return x.unsqueeze(2).to_broadcast([P, T, 2])

            v.tensor_copy(i1T[:], twice(bank[4][:, 0:T]))
            v.tensor_copy(i2T[:], twice(bank[5][:, 0:T]))
            ch.did(v.tensor_copy(gate_parts[:, 0], twice(bank[6][:, 0:T])))
            ch.wait()
            ch.did(v.tensor_tensor(gate_rest[:, 0], bank[6][:, 0:T], gate_parts[:, 0, :, 0], ALU.subtract))
            ch.wait()
            ch.did(v.tensor_copy(gate_parts[:, 1], twice(gate_rest[:, 0])))
            ch.wait()
            ch.did(v.tensor_tensor(gate_parts[:, 2], twice(gate_rest[:, 0]), gate_parts[:, 1], ALU.subtract))
            ch.wait()

            def batch_in(q, n, b, e):
                first = isinstance(n, int) and n == 0
                if not (isinstance(n, int) and n < 2):
                    dve.wait_ge(gb_used, n - 1)
                if not first:
                    dve.wait_ge(gb_ready, n)

                def equal(out, ids, picks, k):
                    shape = [P, GB, k // 2, 2]
                    return v.tensor_tensor(out.rearrange("p t (a d) -> p t a d", d=2),
                                           ids.rearrange("p (a d) -> p a d", d=2).unsqueeze(1).to_broadcast(shape),
                                           picks[:, tokens_of(b)].unsqueeze(2).to_broadcast(shape), ALU.is_equal)

                ch.did(equal(onehot1[:], iota16[:, bass.ds(q * QUARTER, QUARTER)], i1T, QUARTER))
                equal(onehot2[:, e], iota16[:], i2T, P)
                ch.wait()
                shape = [P, GB, QUARTER // 2, 2]
                for part in range(PARTS):
                    last = v.tensor_tensor(gated1[:, e, part].rearrange("p t (a d) -> p t a d", d=2),
                                           onehot1[:].rearrange("p t (a d) -> p t a d", d=2),
                                           gate_parts[:, part, tokens_of(b)].unsqueeze(2).to_broadcast(shape),
                                           ALU.mult)
                last.then_inc(gb_ready, 1)

            for n in range(2):
                batch_in(0, n, n, n)
            with ch.fori(1, BATCHES // 2, 2) as i:
                for e in range(2):
                    batch_in(0, i * 2 + e, i * 2 + e, e)

            for b in range(BANKS):
                dve.wait_ge(bank_free[b], FREED_MAIN)

            def weigh(q, g, rr, r, k):
                o4 = FREED_MAIN + (g - 1) * (OUTS_ROUND // BANKS)
                if k == 0:
                    dve.wait_ge(half_used, RING * r)
                    dve.wait_ge(gb_out, (q + 1) * BATCHES)
                dve.wait_ge(bank_free[k % BANKS], o4 + k // BANKS + 1)
                if k > 1:
                    dve.wait_ge(w_ready, g * GROUP + k - 1)
                gate = gates[:, bass.ds(q % 2, 1), bass.ds(rr * GROUP + k, 1), :].rearrange("p a b t -> p (a b t)")
                ch.did(v.tensor_tensor(pair[:, k % 2], gel[:, k], gate, ALU.mult))
                ch.wait()
                ch.did(v.tensor_copy(wexp_hi[:, k], pair[:, k % 2]))
                ch.wait()
                v.tensor_tensor(wexp_lo[:, k], pair[:, k % 2], wexp_hi[:, k].bitcast(F32), ALU.subtract)\
                    .then_inc(w_ready, 1)

            def add_out(r, k, off, j):
                dve.wait_ge(half_used, RING * r + 2 * k + j % 2 + 1)
                v.tensor_tensor(acc[:, j, :], bank[off % BANKS][:, 0:T], acc[:, j, :], ALU.add)\
                    .then_inc(bank_free[off % BANKS], 1)

            def add_tile(r, k):
                for j in (2 * (k - GROUP), 2 * (k - GROUP) + 1):
                    add_out(r, k, GROUP + j, j)

            def rounds(q, g, rr, build):
                r = W_MAIN // 2 + g * (TILES_ROUND // 2)
                for k in range(TILES_ROUND):
                    ahead(r, k)
                    if k < GROUP:
                        weigh(q, g, rr, r, k)
                    elif k > GROUP:
                        add_tile(r, k - 1)
                    if build and k + 1 in BSLOTS:
                        slot = BSLOTS.index(k + 1)
                        b = rr * len(BSLOTS) + slot
                        batch_in(q + 1, (q + 1) * BATCHES + b, b, slot % 2)
                add_tile(r, TILES_ROUND - 1)

            per_round = 2 * GROUP + len(BSLOTS)
            with ch.fori(0, QUARTERS - 1, GQ * per_round) as q:
                with ch.fori(0, GQ, per_round) as rr:
                    rounds(q, q * GQ + rr, rr, True)
            q = QUARTERS - 1
            with ch.fori(0, GQ - 1, 2 * GROUP) as rr:
                rounds(q, q * GQ + rr, rr, False)
            g = GROUPS - 1
            r = W_MAIN // 2 + g * (TILES_ROUND // 2)
            for k in range(GROUP):
                weigh(q, g, GQ - 1, r, k)
            for k in range(GROUP):
                if k < GROUP - 1:
                    ahead(r, k)
                for j in (2 * k, 2 * k + 1):
                    add_out(r, k, j, j)

            mean_square(1.0 / D, EPS, bank[7][:, 0:T], [(sq_used, 3 * CH)])
            reciprocal_root(HEADS + 3)
            for b in range(4):
                for c in range(4 * b, 4 * b + 4):
                    last = v.scalar_tensor_tensor(out=acc[:, c, :], in0=acc[:, c, :], scalar=gains[:, 2, c:c + 1],
                                                  in1=rstd, op0=ALU.mult, op1=ALU.mult)
                last.then_inc(y_out, 1)


def kernel(x_prompt, x_sample, state_conv, state_ret, norm_mix_g, w_in, conv_w, ret_gn_g, ret_gn_b, w_out,
           norm_ffn_g, peer_w_q, peer_sub_keys, peer_u, peer_v, norm_final_g):
    import concourse.bacc as bacc
    from concourse.bass_utils import run_bass_kernel_spmd

    a = np.asarray
    f = np.float32

    def tiles_of(w, order):
        n_in, n_out = w.shape
        return w.reshape(n_in // P, P, n_out // P, P)[order].transpose(2, 1, 0, 3)

    win = tiles_of(a(w_in)[0], np.arange(CH))
    wout = tiles_of(a(w_out)[0], np.r_[HEADS:2 * HEADS, 0:HEADS])
    wq = tiles_of(a(peer_w_q)[0], np.arange(CH))
    u = a(peer_u)[0].reshape(NK, P, CH, P).transpose(0, 3, 2, 1)
    vv = a(peer_v)[0].reshape(GROUPS, GROUP, P, GROUP, 2, P).transpose(0, 3, 2, 4, 1, 5)
    halves = np.empty((2 * TILES, P, HALF, P), f)

    def put(tile, block):
        n = block.shape[0]
        halves[2 * tile:2 * (tile + n)].reshape(n, 2, P, HALF, P)[:] = \
            block.reshape(n, P, 2, HALF, P).transpose(0, 2, 1, 3, 4)

    put(0, win[CHUNK_ORDER])
    put(W_OUT, wout)
    put(W_Q, wq)
    put(W_U0, u[0:GROUP])
    for g in range(GROUPS):
        at = W_MAIN + g * TILES_ROUND
        if g < GROUPS - 1:
            put(at, u[(g + 1) * GROUP:(g + 2) * GROUP])
            at += GROUP
        put(at, vv[g].reshape(GROUP, P, 2 * GROUP, P))

    def by_chunk(x, n):
        return np.ascontiguousarray(x.reshape(n, P).T)

    x = np.concatenate([a(x_prompt)[0], a(x_sample)[:, 0]])
    arrays = {
        "halves": halves,
        "xT": np.ascontiguousarray(x.reshape(T, CH, P).transpose(2, 1, 0)),
        "conv_state": np.ascontiguousarray(a(state_conv)[0].reshape(NSAMPLE, 2, HEADS, P).transpose(3, 2, 1, 0)),
        "ret_state": np.ascontiguousarray(a(state_ret)[0]),
        "norm_mix": by_chunk(a(norm_mix_g)[0], CH),
        "conv_taps": np.ascontiguousarray(a(conv_w)[0].reshape(3, HEADS, P).transpose(2, 1, 0)),
        "gn_g": by_chunk(a(ret_gn_g)[0], HEADS),
        "gn_b": by_chunk(a(ret_gn_b)[0], HEADS),
        "norm_ffn": by_chunk(a(norm_ffn_g)[0], CH),
        "keysT": np.ascontiguousarray(a(peer_sub_keys)[0].reshape(SETS, NK, P).transpose(2, 0, 1)),
        "norm_fin": by_chunk(a(norm_final_g), CH),
        "shape_constants": shape_constants(),
    }
    nc = bacc.Bacc("TRN2", target_bir_lowering=False, num_devices=1)
    args = [nc.dram_tensor(n, x.shape, F32, kind="ExternalInput").ap() for n, x in arrays.items()]
    outs = (("yT", (P, CH, T)), ("conv_new", (P, HEADS, 2 + 2 * NSAMPLE)), ("ret_prompt", (HEADS, HD, HD)),
            ("ret_sample", (NSAMPLE, HEADS, HD, HD)))
    args += [nc.dram_tensor(n, s, F32, kind="ExternalOutput").ap() for n, s in outs]
    build(nc, *args)
    r = run_bass_kernel_spmd(nc, [arrays], core_ids=[0]).results[0]
    y = r["yT"].transpose(2, 1, 0).reshape(T, D)
    conv = r["conv_new"].transpose(2, 1, 0).reshape(2 + 2 * NSAMPLE, HEADS * P)
    return (y[None, :NPROMPT], y[NPROMPT:, None],
            conv[None, None, 0:2], r["ret_prompt"][None, None],
            np.ascontiguousarray(conv[2:].reshape(2, NSAMPLE, HEADS * P).transpose(1, 0, 2))[None],
            r["ret_sample"][None])
```
